# Optimizing a Trainium2 kernel written in Bass

```python
import math
import jax, jax.numpy as jnp
from jax import lax
import numpy as np

D_MODEL = 1024
BATCH = 1
SEQ = 1024
DEPTH = 1

HEAD_DIM = 64
N_HEADS = 8
N_KV_HEADS = 2
GQA_GROUP = N_HEADS // N_KV_HEADS
WINDOW = 128
BLOCK = 128
ROT_DIM = HEAD_DIM // 4
ROPE_THETA = 500000.0
ATTN_WIDTH = N_HEADS * HEAD_DIM
KV_WIDTH = N_KV_HEADS * HEAD_DIM
CHUNK = 128
G_GROUPS = 8
G_GROUP_DIM = 64
G_WIDTH = G_GROUPS * G_GROUP_DIM
Q_END = ATTN_WIDTH
K_END = Q_END + KV_WIDTH
V_END = K_END + KV_WIDTH
Z_END = V_END + 2 * G_WIDTH
GA_END = Z_END + D_MODEL
IN_COLS = GA_END + D_MODEL
N_GROUPS = 4
EXPERTS_PER_GROUP = 8
N_EXPERTS = N_GROUPS * EXPERTS_PER_GROUP
TOP_K = 2
D_EXPERT = 512
EPS = 1e-5
NEG_INF = -1e30

kernel_name = "hybrid_swa_sink_chunked_gmlp_hier_moe"

def rms_norm(x, g):
    xf = x.astype(jnp.float32)
    y = xf * lax.rsqrt(jnp.mean(xf * xf, axis=-1, keepdims=True) + EPS)
    return (y * g.astype(jnp.float32)).astype(x.dtype)

def layer_norm(x, g, b):
    xf = x.astype(jnp.float32)
    mu = jnp.mean(xf, axis=-1, keepdims=True)
    var = jnp.mean(jnp.square(xf - mu), axis=-1, keepdims=True)
    y = (xf - mu) * lax.rsqrt(var + EPS)
    return (y * g.astype(jnp.float32) + b.astype(jnp.float32)).astype(x.dtype)

def rope_tables(seq):
    inv_freq = ROPE_THETA ** (-jnp.arange(0, ROT_DIM, 2, dtype=jnp.float32) / ROT_DIM)
    pos = jnp.arange(seq, dtype=jnp.float32)
    ang = pos[:, None] * inv_freq[None, :]
    return jnp.cos(ang), jnp.sin(ang)

def partial_rope(t, cos, sin):
    tr, tp = t[..., :ROT_DIM], t[..., ROT_DIM:]
    t1 = tr[..., :ROT_DIM // 2].astype(jnp.float32)
    t2 = tr[..., ROT_DIM // 2:].astype(jnp.float32)
    c = cos[None, :, None, :]
    s = sin[None, :, None, :]
    rot = jnp.concatenate([t1 * c - t2 * s, t2 * c + t1 * s], axis=-1)
    return jnp.concatenate([rot.astype(t.dtype), tp], axis=-1)

def sliding_window_sink_attention(q, k, v, sinks):
    b, s = q.shape[0], q.shape[1]
    nb = s // BLOCK
    q = q.reshape(b, nb, BLOCK, N_KV_HEADS, GQA_GROUP, HEAD_DIM)
    k = k.reshape(b, nb, BLOCK, N_KV_HEADS, HEAD_DIM)
    v = v.reshape(b, nb, BLOCK, N_KV_HEADS, HEAD_DIM)
    prev = lambda t: jnp.concatenate([jnp.zeros_like(t[:, :1]), t[:, :-1]], axis=1)
    kk = jnp.concatenate([prev(k), k], axis=2)
    vv = jnp.concatenate([prev(v), v], axis=2)
    scores = jnp.einsum("bnqhgd,bnkhd->bnhgqk", q, kk,
                        preferred_element_type=jnp.float32) * (1.0 / math.sqrt(HEAD_DIM))
    qi = jnp.arange(BLOCK)[:, None]
    kj = jnp.arange(2 * BLOCK)[None, :]
    rel = qi + BLOCK - kj
    band = (rel >= 0) & (rel < WINDOW)
    has_prev = (jnp.arange(nb) > 0)[:, None, None] | (kj >= BLOCK)[None]
    valid = band[None] & has_prev
    scores = jnp.where(valid[None, :, None, None], scores, NEG_INF)
    sink = jnp.broadcast_to(
        sinks.astype(jnp.float32).reshape(N_KV_HEADS, GQA_GROUP)[None, None, :, :, None, None],
        scores.shape[:-1] + (1,))
    probs = jax.nn.softmax(jnp.concatenate([scores, sink], axis=-1), axis=-1)[..., :-1]
    out = jnp.einsum("bnhgqk,bnkhd->bnqhgd", probs.astype(vv.dtype), vv)
    return out.reshape(b, s, ATTN_WIDTH)

def chunked_spatial_gating(z, ln_g, ln_b, w_s, b_s):
    b, s = z.shape[0], z.shape[1]
    nc = s // CHUNK
    u, v = z[..., :G_WIDTH], z[..., G_WIDTH:]
    v = layer_norm(v, ln_g, ln_b).reshape(b, nc, CHUNK, G_GROUPS, G_GROUP_DIM)
    causal = jnp.tril(jnp.ones((CHUNK, CHUNK), dtype=w_s.dtype))
    w = w_s * causal[None]
    mixed = jnp.einsum("gqp,bcpgd->bcqgd", w, v) + b_s.T[None, None, :, :, None]
    return u * mixed.reshape(b, s, G_WIDTH)

def hierarchical_moe(h, wg, bg, we, be, w_gate, w_up, w_down):
    b, s, d = h.shape
    t = h.reshape(b * s, d)
    g_logits = (t @ wg).astype(jnp.float32) + bg.astype(jnp.float32)
    g_prob = jax.nn.softmax(g_logits, axis=-1)
    g_sel = jnp.argmax(g_prob, axis=-1)
    g_w = jnp.take_along_axis(g_prob, g_sel[:, None], axis=-1)
    e_logits = ((t @ we).astype(jnp.float32) + be.astype(jnp.float32)).reshape(-1, N_GROUPS, EXPERTS_PER_GROUP)
    e_in_group = jnp.take_along_axis(e_logits, g_sel[:, None, None], axis=1)[:, 0]
    top_logit, top_idx = lax.top_k(e_in_group, TOP_K)
    weights = g_w * jax.nn.softmax(top_logit, axis=-1)
    expert_id = (g_sel[:, None] * EXPERTS_PER_GROUP + top_idx).reshape(-1)
    order = jnp.argsort(expert_id)
    tok = order // TOP_K
    xs = t[tok]
    ws = weights.reshape(-1)[order]
    sizes = jnp.bincount(expert_id, length=N_EXPERTS).astype(jnp.int32)
    hid = jax.nn.silu(lax.ragged_dot(xs, w_gate, sizes)) * lax.ragged_dot(xs, w_up, sizes)
    ys = lax.ragged_dot(hid, w_down, sizes) * ws[:, None].astype(hid.dtype)
    out = jnp.zeros_like(t).at[tok].add(ys.astype(t.dtype))
    return out.reshape(b, s, d)

def setup_inputs(seed: int = 0) -> dict:
    key = jax.random.key(seed)
    ks = jax.random.split(key, 24)
    n = lambda k, shape, scale: jax.random.normal(k, shape, jnp.float32) * scale
    return {
        "x": n(ks[0], (BATCH, SEQ, D_MODEL), 1.0),
        "norm1_g": 1.0 + n(ks[1], (DEPTH, D_MODEL), 0.05),
        "w_in": n(ks[2], (DEPTH, D_MODEL, IN_COLS), D_MODEL ** -0.5),
        "attn_sinks": n(ks[3], (DEPTH, N_HEADS), 1.0),
        "gmlp_ln_g": 1.0 + n(ks[4], (DEPTH, G_WIDTH), 0.05),
        "gmlp_ln_b": n(ks[5], (DEPTH, G_WIDTH), 0.05),
        "gmlp_ws": n(ks[6], (DEPTH, G_GROUPS, CHUNK, CHUNK), CHUNK ** -0.5),
        "gmlp_bs": 1.0 + n(ks[7], (DEPTH, G_GROUPS, CHUNK), 0.1),
        "w_attn_branch": n(ks[8], (DEPTH, ATTN_WIDTH, D_MODEL), ATTN_WIDTH ** -0.5),
        "w_gmlp_branch": n(ks[9], (DEPTH, G_WIDTH, D_MODEL), G_WIDTH ** -0.5),
        "w_out": n(ks[10], (DEPTH, D_MODEL, D_MODEL), D_MODEL ** -0.5),
        "norm2_g": 1.0 + n(ks[11], (DEPTH, D_MODEL), 0.05),
        "router_group_w": n(ks[12], (DEPTH, D_MODEL, N_GROUPS), D_MODEL ** -0.5),
        "router_group_b": n(ks[13], (DEPTH, N_GROUPS), 0.01),
        "router_expert_w": n(ks[14], (DEPTH, D_MODEL, N_EXPERTS), D_MODEL ** -0.5),
        "router_expert_b": n(ks[15], (DEPTH, N_EXPERTS), 0.01),
        "expert_w_gate": n(ks[16], (DEPTH, N_EXPERTS, D_MODEL, D_EXPERT), D_MODEL ** -0.5),
        "expert_w_up": n(ks[17], (DEPTH, N_EXPERTS, D_MODEL, D_EXPERT), D_MODEL ** -0.5),
        "expert_w_down": n(ks[18], (DEPTH, N_EXPERTS, D_EXPERT, D_MODEL), D_EXPERT ** -0.5),
        "final_norm_g": 1.0 + n(ks[19], (D_MODEL,), 0.05),
    }

def reference(x, norm1_g, w_in, attn_sinks, gmlp_ln_g, gmlp_ln_b, gmlp_ws, gmlp_bs,
              w_attn_branch, w_gmlp_branch, w_out, norm2_g, router_group_w, router_group_b,
              router_expert_w, router_expert_b, expert_w_gate, expert_w_up, expert_w_down,
              final_norm_g):
    b, s, _ = x.shape
    cos, sin = rope_tables(s)
    for l in range(DEPTH):
        h = rms_norm(x, norm1_g[l])
        proj = h @ w_in[l]
        q, k, v, z, ga, gg = jnp.split(proj, [Q_END, K_END, V_END, Z_END, GA_END], axis=-1)
        q = partial_rope(q.reshape(b, s, N_HEADS, HEAD_DIM), cos, sin)
        k = partial_rope(k.reshape(b, s, N_KV_HEADS, HEAD_DIM), cos, sin)
        v = v.reshape(b, s, N_KV_HEADS, HEAD_DIM)
        a = sliding_window_sink_attention(q, k, v, attn_sinks[l]) @ w_attn_branch[l]
        g = chunked_spatial_gating(jax.nn.gelu(z), gmlp_ln_g[l], gmlp_ln_b[l],
                                   gmlp_ws[l], gmlp_bs[l]) @ w_gmlp_branch[l]
        mixed = jax.nn.sigmoid(ga) * a + jax.nn.sigmoid(gg) * g
        x = x + mixed @ w_out[l]
        x = x + hierarchical_moe(rms_norm(x, norm2_g[l]), router_group_w[l], router_group_b[l],
                                 router_expert_w[l], router_expert_b[l], expert_w_gate[l],
                                 expert_w_up[l], expert_w_down[l])
    return rms_norm(x, final_norm_g)


_drawn_inputs = setup_inputs


def setup_inputs(seed=0):
    import zlib

    import numpy as np

    out = dict(_drawn_inputs(seed))
    spreads = {}
    factors = {'attn_sinks': 6.922, 'router_group_b': 5.232, 'router_expert_b': 4.779}
    for name, (base, spread) in spreads.items():
        noise = np.random.default_rng([zlib.crc32(name.encode()), seed]).standard_normal(out[name].shape)
        drawn = base * np.exp(spread * noise) if base else spread * noise
        out[name] = __import__('jax').numpy.asarray(drawn.astype(out[name].dtype))
    for name, factor in factors.items():
        out[name] = (out[name] * factor).astype(out[name].dtype)
    return out
```

```python
from contextlib import ExitStack

import numpy as np

import concourse.bass as bass
from concourse import mybir

F32 = mybir.dt.float32
F32R = mybir.dt.float32r
BF16 = mybir.dt.bfloat16
I32 = mybir.dt.int32
ACT = mybir.ActivationFunctionType
ALU = mybir.AluOpType
AX_X = mybir.AxisListType.X

P = 128
SEQ = 1024
D = 1024
KT = D // P
TILES = SEQ // P
HEADS, KV_HEADS, HD = 8, 2, 64
PAIRS = HEADS // KV_HEADS
ROT = HD // 4
QKV = HEADS * HD + 2 * KV_HEADS * HD
GW = 512
GROUPS = 8
Z_U0 = QKV
Z_V0 = Z_U0 + GW
GA0 = Z_V0 + GW
GG0 = GA0 + D
IN_COLS = GG0 + D
N_GRP, PER_GRP = 4, 8
NE = N_GRP * PER_GRP
F = 512
EPS = 1e-5
NEG = -1e30
HALF = 512
SLAB = 2048
RAW_SLOTS, SPLIT_SLOTS = 3, 6
MORE_SLOTS = 3
MAX_OVER = 2 * SEQ // P - 1
ITEMS = NE + MAX_OVER
GPAD = 8
LOGITS = GPAD + NE
FAR = 4096

SLAB_A, SLAB_B, SLAB_C0, SLAB_C1, SLAB_E0, SLAB_E1, SLAB_O, SLAB_X = 0, 3, 7, 10, 13, 16, 19, 23
SLAB_WIDE = SLAB_X + 4
SLAB_TAIL = SLAB_X + 6 * NE - 2
SLAB_OVER = SLAB_TAIL + 2

C_ID, C_SLOT, C_TRI, C_COS, C_SIN = 0, 128, 256, 384, 512
C_GROUP, C_IOTA32, C_P, C_TILE, C_J = 640, 672, 704, 705, 713
C_END = C_J + MAX_OVER + 1
M_CAUSAL = 5 * 256
M_END = M_CAUSAL + 128


def constants():
    c = np.zeros((P, C_END), np.float32)
    p = np.arange(P)
    c[:, C_ID:C_ID + P] = np.eye(P)
    c[:, C_SLOT:C_SLOT + P] = p[None] + 1
    c[:, C_TRI:C_TRI + P] = p[:, None] < p[None]
    inv = np.float32(500000.0) ** (-np.arange(0, ROT, 2, dtype=np.float32) / np.float32(ROT))
    ang = np.arange(SEQ, dtype=np.float32)[:, None] * inv[None].astype(np.float32)
    cos, sin = np.cos(ang), np.sin(ang)
    c[:, C_COS:C_COS + P] = np.concatenate([cos, cos], 1).reshape(TILES, P, ROT).transpose(1, 0, 2).reshape(P, -1)
    c[:, C_SIN:C_SIN + P] = np.concatenate([-sin, sin], 1).reshape(TILES, P, ROT).transpose(1, 0, 2).reshape(P, -1)
    c[:, C_GROUP:C_GROUP + NE] = np.arange(NE) // PER_GRP
    c[:, C_IOTA32:C_IOTA32 + NE] = np.arange(NE)
    c[:, C_P] = p
    c[:, C_TILE:C_TILE + TILES] = P * np.arange(TILES) - FAR
    c[:, C_J:C_J + MAX_OVER + 1] = np.arange(MAX_OVER + 1)
    m = np.zeros((P, M_END), np.float32)
    now = np.where(p[:, None] >= p[None], 0, NEG)
    before = np.where(p[:, None] < p[None], 0, NEG)
    for n in range(4):
        m[:, n * 256:n * 256 + 128] = now
        m[:, n * 256 + 128:n * 256 + 256] = before if n else NEG
    m[:, 1024:1152], m[:, 1152:1280] = before, now
    m[:, M_CAUSAL:] = p[:, None] <= p[None]
    return c, m


def wait(eng, sem, count):
    if type(count) is int and count <= 0:
        return
    eng.wait_ge(sem, count)


def wait_apart(eng, sem, count, carrier, more=()):
    for s, c in [(sem, count), *more]:
        wait(eng, s, c)
    if type(count) is not int:
        carrier()


def over_tiles(eng, body, between=(), before_last=None):
    body(0, 0, True, False)
    for work in between[:1]:
        work()
    body(0, 1, False, False)
    for work in between[1:]:
        work()
    with eng.Fori(1, TILES // 2 - 1) as pair:
        body(pair, 0, False, False)
        body(pair, 1, False, False)
    if before_last:
        before_last()
    body(TILES // 2 - 1, 0, False, False)
    body(TILES // 2 - 1, 1, False, True)


def build(nc, x, norm1_g, w_in, attn_sinks, gmlp_ln_g, gmlp_ln_b, gmlp_ws, gmlp_bs, w_attn_branch,
          w_gmlp_branch, w_out, norm2_g, router_group_w, router_group_b, router_expert_w,
          router_expert_b, expert_w_gate, expert_w_up, expert_w_down, final_norm_g, consts, masks,
          out):
    def scratch(name, cols):
        return nc.dram_tensor(name, (SEQ, cols), F32, kind="Internal").ap()

    qkv_d = scratch("qkv_d", QKV)
    z_d = scratch("z_d", 2 * GW)
    ao_d = scratch("ao_d", HEADS * HD)
    g_d = scratch("g_d", GW)
    am_d = scratch("am_d", D)
    mixed_d = scratch("mixed_d", D)
    h2_d = scratch("h2_d", D)
    acc_d = scratch("acc_d", D)

    x_rows = x[0]
    out_rows = out[0]
    win = w_in[0].rearrange("(k p) n -> p k n", p=P)
    wab = w_attn_branch[0].rearrange("(k p) n -> p k n", p=P)
    wgb = w_gmlp_branch[0].rearrange("(k p) n -> p k n", p=P)
    wo = w_out[0].rearrange("(k p) n -> p k n", p=P)
    slabs = [win[:, 0:4, 0:HALF], win[:, :, HALF:QKV], win[:, 4:8, 0:HALF]]
    for h in range(2):
        for c0 in (Z_V0, Z_U0):
            slabs.append(win[:, 4 * h:4 * h + 4, c0:c0 + HALF])
    for c0, branch in ((GA0, wab), (GG0, wgb)):
        for c in range(2):
            lo, hi = c * HALF, (c + 1) * HALF
            slabs += [win[:, 0:4, c0 + lo:c0 + hi], win[:, 4:8, c0 + lo:c0 + hi], branch[:, :, lo:hi]]
    for h in range(2):
        for c in range(2):
            slabs.append(wo[:, 4 * h:4 * h + 4, c * HALF:(c + 1) * HALF])
    assert len(slabs) == SLAB_X

    with ExitStack() as ctx:
        def sb(name, shape, dt=F32):
            return ctx.enter_context(nc.sbuf_tensor(name, shape, dt))

        def ps(name, shape, dt=F32):
            return ctx.enter_context(nc.psum_tensor(name, shape, dt))

        def sem(name):
            return ctx.enter_context(nc.semaphore(name))

        raw = sb("raw", [P, RAW_SLOTS, SLAB])
        whi = sb("whi", [P, SPLIT_SLOTS, SLAB], F32R)
        wlo = sb("wlo", [P, SPLIT_SLOTS, SLAB], F32R)
        sth = sb("sth", [P, KT, P], F32R)
        stl = sb("stl", [P, KT, P], F32R)
        bth = sb("bth", [P, 4, P], F32R)
        btl = sb("btl", [P, 4, P], F32R)
        xgt = sb("xgt", [P, KT, SEQ])
        arena = sb("arena", [P, 6144])
        con = sb("con", [P, C_END])
        maskb = sb("maskb", [P, 5, 256], BF16)
        identb = sb("identb", [P, P], BF16)
        trib = sb("trib", [P, P], BF16)
        onesb = sb("onesb", [P, P], BF16)
        wsT = sb("wsT", [P, GROUPS, P])
        chan = sb("chan", [P, 2, GW])
        router_w = sb("router_w", [P, KT, LOGITS])
        router_b = sb("router_b", [P, LOGITS])
        g1 = sb("g1", [P, KT])
        bs = sb("bs", [P, GROUPS])
        sinks = sb("sinks", [P, HEADS])
        nsinks = sb("nsinks", [P, HEADS])
        nmax = sb("nmax", [P, HEADS])
        esum = sb("esum", [P, HEADS])
        sinke = sb("sinke", [P, HEADS])
        rden = sb("rden", [P, HEADS])
        mhalf = sb("mhalf", [P, 1])
        epsc = sb("epsc", [P, 1])
        scrap = sb("scrap", [P, 8])
        scrap_a = sb("scrap_a", [P, 1])
        meansq = sb("meansq", [P, 2])
        rstd = sb("rstd", [P, TILES])
        hrstd = sb("hrstd", [P, TILES])
        rstd2 = sb("rstd2", [P, 2])
        lnst = sb("lnst", [P, 6])
        lnmv = sb("lnmv", [P, 2, 2])
        lnrs = sb("lnrs", [P, 2])
        ident = con[:, C_ID:C_ID + P]

        pX = ps("pX", [P, 2, HALF])
        pA = [ps("pA0", [P, 2, HALF]), ps("pA1", [P, 2, HALF])]
        p6 = ps("p6", [P, HALF])
        p7 = ps("p7", [P, HALF])

        def area(base, at, *shape):
            n = int(np.prod(shape))
            v = base[:, at:at + n]
            if len(shape) == 1:
                return v
            names = "abc"[:len(shape)]
            return v.rearrange(f"p ({' '.join(names)}) -> p {' '.join(names)}", **dict(zip(names, shape)))

        a_x = area(arena, 0, 2, D)
        a_junk = area(arena, 2048, 512).bitcast(BF16)
        a_rot = area(arena, 2560, 2, 160)
        a_qkv = area(arena, 2880, 2, QKV)
        m_in = area(arena, 4416, M_END)
        b_qT = area(arena, 0, PAIRS, P)
        b_kT = area(arena, 512, KV_HEADS, 2 * P)
        b_p = area(arena, 1024, 2, 512)
        b_pT = area(arena, 2048, 2, 512)
        b_z = area(arena, 3072, 2, GW)
        b_qkv = area(arena, 4608, 2, QKV)
        b_v = sb("b_v", [P, 2, P])
        b_out = sb("b_out", [P, HEADS * HD])
        c_src = [area(arena, 4608, HALF), area(arena, 1024, HALF)]
        c_z = [area(arena, 5120, 2 * GW), area(arena, 0, 2 * GW)]
        c_out = area(arena, 1536, 2, HALF)
        c_g = area(arena, 2560, 2, GW)
        o_mix = area(arena, 2560, 2, D)
        late = xgt[:, :, :].rearrange("p k t -> p (k t)")
        o_h2T = area(late, 1024, KT, P)
        o_h2 = area(late, 2048, D)
        o_x = [area(late, 0, D), area(late, 3072, D)]
        o_x2 = area(late, 4096, D)
        e_xs = area(late, 0, D)
        e_y = area(late, 1024, D)
        e_hid = area(late, 2048, F)
        e_sil = area(late, 2560, F)
        gf = area(late, 3072, D)
        e_hot = area(late, 4096, 512).bitcast(BF16).rearrange("p (i s) -> p i s", i=TILES)
        route = area(late, 5792, ITEMS * TILES * 5 // 2).bitcast(BF16).rearrange("p (m i c) -> p m i c", m=ITEMS, i=TILES)
        pos = area(late, 4608, ITEMS, TILES)
        junk = area(late, 5280, 512).bitcast(BF16)
        passed = area(late, 5280, MAX_OVER + 1, NE)
        chosen = area(late, 6736, TILES * NE // 2).bitcast(BF16).rearrange("p (i e) -> p i e", e=NE)
        csum = area(late, 6864, (TILES + 1) * NE // 2).bitcast(BF16).rearrange("p (i e) -> p i e", e=NE)
        lg = area(late, 7008, 2, LOGITS)
        ev, gmask, hot1 = (area(late, 7088 + NE * n, NE) for n in range(3))
        wq = area(late, 7184, 3, NE)
        g8, gi8, gidx = area(late, 7280, 8), area(late, 7288, 8).bitcast(mybir.dt.uint32), area(late, 7296, 1)
        e8 = area(late, 7304, 2, 8)
        ei8 = area(late, 7320, 8).bitcast(mybir.dt.uint32)
        eidx = area(late, 7328, 2, 2)
        ntop = area(late, 7332, 2, 2)
        gsum, ex = area(late, 7336, 2, 1), area(late, 7338, 2, 1)
        gexp = area(late, 7340, N_GRP)
        wts = area(late, 7344, 4)
        mone = area(late, 7348, 1)
        over, ends, other, count = (area(late, 7352 + NE * n, NE) for n in range(4))
        small = area(late, 7480, 64)
        raw_slots = [raw[:, n, :] for n in range(RAW_SLOTS)] + [area(arena, n * SLAB, SLAB) for n in range(MORE_SLOTS)]
        f_x = [raw_slots[t // 2][:, (t % 2) * D:(t % 2 + 1) * D] for t in range(TILES)]
        e_ws = sb("e_ws", [P, ITEMS])
        e_row = sb("e_row", [P, ITEMS], I32)
        e_tab = sb("e_tab", [P, 5])
        e_grow = sb("e_grow", [P, 1], I32)
        e_srow = sb("e_srow", [P, 1], I32)
        e_pos = sb("e_pos", [P, TILES])
        over_e = sb("over_e", [P, MAX_OVER + 1])
        over_shift = sb("over_shift", [P, MAX_OVER + 1])
        over_ei = sb("over_ei", [P, MAX_OVER + 1], I32)
        over_n = sb("over_n", [P, 1], I32)
        o_sel = area(late, 7552, NE)

        raw_in = [sem(f"raw_in{n}") for n in range(RAW_SLOTS + MORE_SLOTS)]
        hi_conv, lo_conv, slab_free = sem("hi_conv"), sem("lo_conv"), sem("slab_free")
        hi_half, lo_half, half_free = sem("hi_half"), sem("lo_half"), sem("half_free")
        ident_in, con_in, g1_in, mask_in, ws_in, small_in, chan_in, g2_in, gf_in = (sem(n) for n in (
            "ident_in", "con_in", "g1_in", "mask_in", "ws_in", "small_in", "chan_in", "g2_in", "gf_in"))
        setup_done, ws_turned, ws_copied, mh_set = sem("setup_done"), sem("ws_turned"), sem("ws_copied"), sem("mh_set")
        x_in = [sem("x_in0"), sem("x_in1")]
        x_turned, xgt_done, sq_done, eps_done, rstd_done = (sem(n) for n in (
            "x_turned", "xgt_done", "sq_done", "eps_done", "rstd_done"))
        tile_done, act_evac, dve_evac, rope_done = (sem(n) for n in ("tile_done", "act_evac", "dve_evac", "rope_done"))
        qkv_out = [sem("qkv_out0"), sem("qkv_out1")]
        qkv_in = [sem("qkv_in0"), sem("qkv_in1")]
        qk_turned, qT_done, kT_done, s_done, nmax_done, exp_done, p_turned, pT_done, pv_done, o_done = (sem(n) for n in (
            "qk_turned", "qT_done", "kT_done", "s_done", "nmax_done", "exp_done", "p_turned", "pT_done", "pv_done", "o_done"))
        sink_arg, sink_exp, zv_done, zv_read, hrstd_done = (sem(n) for n in (
            "sink_arg", "sink_exp", "zv_done", "zv_read", "hrstd_done"))
        z_out = [sem("z_out0"), sem("z_out1")]
        ao_out = [sem("ao_out0"), sem("ao_out1")]
        src_in = [sem("src_in0"), sem("src_in1")]
        z_in = [sem("z_in0"), sem("z_in1")]
        am_in = [sem("am_in0"), sem("am_in1")]
        g_out = [sem("g_out0"), sem("g_out1")]
        gate_out = [sem("gate_out0"), sem("gate_out1")]
        src_turned, hi_src, lo_src = (sem(n) for n in ("src_turned", "hi_src", "lo_src"))
        gelu_done, ln_stat, ln_eps, ln_rstd, ln_done, mix_done, g_done = (sem(n) for n in (
            "gelu_done", "ln_stat", "ln_eps", "ln_rstd", "ln_done", "mix_done", "g_done"))
        mix_in = [sem("mix_in0"), sem("mix_in1")]
        ox_in = [sem("ox_in0"), sem("ox_in1")]
        mix_turned, x2_done, sq2_done, eps2_done, rstd2_done, h2_done, h2_turned, h2T_done, log_done, log_read = (sem(n) for n in (
            "mix_turned", "x2_done", "sq2_done", "eps2_done", "rstd2_done", "h2_done", "h2_turned", "h2T_done", "log_done", "log_read"))
        acc_out, h2_out = sem("acc_out"), sem("h2_out")
        route_set, top_done, exps_done, ranks_done, pos_done, w_done, over_listed = (sem(n) for n in (
            "route_set", "top_done", "exps_done", "ranks_done", "pos_done", "w_done", "over_listed"))
        pos_copied, hot_done, tab_done, tab_read, row_copied, xs_in, xs_turned, hi_xs, lo_xs = (sem(n) for n in (
            "pos_copied", "hot_done", "tab_done", "tab_read", "row_copied", "xs_in", "xs_turned", "hi_xs", "lo_xs"))
        sil_done, hid_done, hid_turned, hi_hid, lo_hid, y_done, srow_copied, y_out = (sem(n) for n in (
            "sil_done", "hid_done", "hid_turned", "hi_hid", "lo_hid", "y_done", "srow_copied", "y_out"))
        over_pos = sem("over_pos")
        f_in, f_out, moe_done = [sem(f"f_in{n}") for n in range(TILES)], sem("f_out"), sem("moe_done")
        f_sq, f_eps, f_rstd, f_norm = sem("f_sq"), sem("f_eps"), sem("f_rstd"), sem("f_norm")

        def half_no(stage, t, h):
            return 16 * stage + 2 * t + h

        def expert_slab(e, j):
            if type(e) is int and e == 0:
                return SLAB_X + j, 0
            if type(e) is int and e == NE:
                return SLAB_TAIL + j - 4, 0
            return SLAB_X - 2 + j, e

        def over_slab(item, j):
            return SLAB_OVER + j, item

        def freed(base, times=0):
            return base + times * 6 + 1

        def gate_count(m, item):
            return freed(*(expert_slab(m, 1) if item is None else over_slab(item, 1)))

        def up_count(m, item):
            return freed(*(expert_slab(m, 3) if item is None else over_slab(item, 3)))

        def down_count(m, item):
            return freed(*(expert_slab(m + 1, 5) if item is None else over_slab(item, 5)))

        def before(count, m, item):
            if item is not None:
                return SLAB_OVER + item * 6
            return 0 if type(m) is int and m == 0 else count(m - 1, None)

        def rows(t):
            return bass.ds(t * P, P)

        def raw_slot(base, times):
            wide = RAW_SLOTS + MORE_SLOTS
            if type(times) is int and base + 6 * times < SLAB_WIDE:
                n = base + 6 * times
                return n % RAW_SLOTS, n // RAW_SLOTS + 1, RAW_SLOTS
            slot = base % wide
            if slot >= RAW_SLOTS:
                return slot, (base - SLAB_WIDE) // wide + 1 + times, wide
            return slot, SLAB_WIDE // RAW_SLOTS + (base - SLAB_WIDE - MORE_SLOTS) // wide + 1 + times, wide

        def split_hi(act, base, times=0):
            slot, uses, _ = raw_slot(base, times)
            wait(act, raw_in[slot], uses * 16)
            wait(act, slab_free, base + times * 6 - SPLIT_SLOTS + 1)
            nc.scalar.activation(whi[:, base % SPLIT_SLOTS, :], raw_slots[slot], ACT.Copy).then_inc(hi_conv, 1)

        def split_lo(dve, base, times=0):
            slot, uses, _ = raw_slot(base, times)
            wait(dve, raw_in[slot], uses * 16)
            wait(dve, slab_free, base + times * 6 - SPLIT_SLOTS + 1)
            wait(dve, hi_conv, base + times * 6 + 1)
            nc.vector.tensor_sub(wlo[:, base % SPLIT_SLOTS, :], raw_slots[slot],
                                 whi[:, base % SPLIT_SLOTS, :].bitcast(F32)).then_inc(lo_conv, 1)

        def slab_ready(pe, base, times=0):
            wait(pe, hi_conv, base + times * 6 + 1)
            wait(pe, lo_conv, base + times * 6 + 1)

        def product(out_ap, hi, lo, base, col, width, k, k_slab, first, last):
            s = base % SPLIT_SLOTS
            at = k_slab * width[0] + col
            wh, wl = whi[:, s, at:at + width[1]], wlo[:, s, at:at + width[1]]
            nc.tensor.matmul(out_ap, hi[:, k, :], wh, start=first, stop=False)
            nc.tensor.matmul(out_ap, hi[:, k, :], wl, start=False, stop=False)
            return nc.tensor.matmul(out_ap, lo[:, k, :], wh, start=False, stop=last)

        def slabs_of_b(pair, u):
            return {(0, 0): [6], (0, 1): [7], (TILES // 2 - 1, 0): [8]}.get((pair, u), []) if type(pair) is int else []

        block = ctx.enter_context(nc.Block())

        @block.sync
        def _(sp):
            def load(src, base, times=0):
                slot, _, ring = raw_slot(base, times)
                wait(sp, hi_conv, base + times * 6 - ring + 1)
                wait(sp, lo_conv, base + times * 6 - ring + 1)
                dst = raw_slots[slot].rearrange("p (k n) -> p k n", n=src.shape[-1])
                sp.dma_start(dst, src).then_inc(raw_in[slot], 16)

            def expert(w, e, j):
                rows_ = SLAB // w.shape[-1] * P
                return w[0, bass.ds(e, 1), j * rows_:(j + 1) * rows_, :].rearrange("a (k p) n -> p (a k) n", p=P)

            def load_slabs(*numbers):
                for n in numbers:
                    if n < SLAB_X:
                        load(slabs[n], n)
                    else:
                        e, j = (0, n - SLAB_X) if n < SLAB_X + 4 else (1, n - SLAB_X - 4)
                        load(expert((expert_w_gate, expert_w_up)[j // 2], e, j % 2), n)

            def ahead(t):
                return not (type(t) is int and t > TILES - 3)

            sp.dma_start(a_x[:, 0, :], x_rows[0:P, :]).then_inc(x_in[0], 16)
            load_slabs(0, 1)
            sp.dma_start(a_x[:, 1, :], x_rows[P:2 * P, :]).then_inc(x_in[1], 16)
            load_slabs(2)
            sp.dma_start(con[:, P:], consts[:, P:]).then_inc(con_in, 16)
            load_slabs(3)
            sp.wait_ge(x_turned, 1)
            sp.wait_ge(sq_done, 1)
            sp.dma_start(a_x[:, 0, :], x_rows[2 * P:3 * P, :]).then_inc(x_in[0], 16)
            load_slabs(4, 5)

            def load_qkv(t, u, count):
                wait(sp, qkv_out[u], count)
                sp.dma_start(b_qkv[:, u, :], qkv_d[rows(t), :]).then_inc(qkv_in[u], 16)

            def stage_a(pair, u, first, last):
                t = 2 * pair + u
                if ahead(t) and not first:
                    wait(sp, x_turned, t + 1)
                    wait(sp, sq_done, t + 1)
                    sp.dma_start(a_x[:, u, :], x_rows[rows(t + 2), :]).then_inc(x_in[u], 16)
                wait(sp, rope_done, t + 1)
                sp.dma_start(qkv_d[rows(t), :], a_qkv[:, u, :]).then_inc(qkv_out[u], 16)

            def prepare_b():
                load_slabs(6, 7)
                sp.wait_ge(setup_done, 1)
                load_qkv(0, 0, 16)
                load_qkv(1, 1, 16)

            over_tiles(sp, stage_a, before_last=prepare_b)
            load_slabs(8)

            def load_src(c_stage, t, u, pair):
                if c_stage >= 2:
                    wait(sp, g_out[u], 16 * pair + 16)
                else:
                    wait(sp, ao_out[u], 16 * pair + 16)
                sp.dma_start(c_src[u], (g_d if c_stage >= 2 else ao_d)[rows(t), :]).then_inc(src_in[u], 16)

            def load_z(t, u, pair):
                wait(sp, z_out[u], 16 * pair + 16)
                sp.dma_start(c_z[u], z_d[rows(t), :]).then_inc(z_in[u], 16)

            def load_sum(c_stage, t, u, pair):
                wait(sp, gate_out[u], 64 * (c_stage - 2) + 16 * pair + 16)
                col = (c_stage - 2) * HALF
                sp.dma_start(c_z[u][:, 0:HALF], am_d[rows(t), col:col + HALF]).then_inc(am_in[u], 16)

            def stage_b(pair, u, first, last):
                t = 2 * pair + u
                if ahead(t):
                    wait(sp, kT_done, t + 1)
                    load_qkv(t + 2, u, 16 * pair + 32)
                if last:
                    sp.wait_ge(kT_done, TILES)
                    load_src(0, 0, 0, 0)
                    load_z(0, 0, 0)
                wait(sp, act_evac, TILES + t + 1)
                sp.dma_start(z_d[rows(t), :], b_z[:, :, :].rearrange("p a n -> p (a n)")).then_inc(z_out[u], 16)
                if last:
                    sp.wait_ge(p_turned, 4 * TILES)
                    load_src(0, 1, 1, 0)
                    load_z(1, 1, 0)
                wait(sp, o_done, t + 1)
                sp.dma_start(ao_d[rows(t), :], b_out[:]).then_inc(ao_out[u], 16)

            over_tiles(sp, stage_b, before_last=lambda: load_slabs(9, 10))
            load_slabs(11)

            def load_mix(t, u):
                sp.dma_start(o_mix[:, u, :], mixed_d[rows(t), :]).then_inc(mix_in[u], 16)

            for c_stage in range(4):
                gmlp, adds, col = c_stage == 0, c_stage >= 2, (c_stage % 2) * HALF
                base = 8 * c_stage
                dst_d = mixed_d if adds else am_d

                def stage_c(pair, u, first, last):
                    t = 2 * pair + u
                    if ahead(t):
                        wait(sp, src_turned, base + t + 1)
                        load_src(c_stage, t + 2, u, pair + 1)
                    elif c_stage < 3:
                        wait(sp, src_turned, base + t + 1)
                        load_src(c_stage + 1, u, u, 0)
                    else:
                        wait(sp, gate_out[u], 64 * 3 + 16)
                        load_mix(u, u)
                    if gmlp:
                        wait(sp, g_done, t + 1)
                        sp.dma_start(g_d[rows(t), :], c_g[:, u, :]).then_inc(g_out[u], 16)
                        if ahead(t):
                            load_z(t + 2, u, pair + 1)
                    wait(sp, dve_evac, base + t + 1)
                    sp.dma_start(dst_d[rows(t), col:col + HALF], c_out[:, u, :]).then_inc(gate_out[u], 16)
                    if adds and ahead(t):
                        load_sum(c_stage, t + 2, u, pair + 1)
                    if not ahead(t) and c_stage in (1, 2):
                        load_sum(c_stage + 1, u, u, 0)

                n0 = (SLAB_C1, SLAB_E0, SLAB_E1, SLAB_O)[c_stage] + 3
                over_tiles(sp, stage_c, [lambda: load_slabs(12)] if gmlp else [],
                           before_last=lambda: load_slabs(n0, n0 + 1))
                load_slabs(n0 + 2)

            def load_ox(t, u):
                sp.dma_start(o_x[u], x_rows[rows(t), :]).then_inc(ox_in[u], 16)

            load_ox(0, 0)
            for u in range(2):
                sp.wait_ge(gate_out[u], 16 * 16)
            load_ox(1, 1)

            def stage_o(pair, u, first, last):
                t = 2 * pair + u
                if ahead(t):
                    wait(sp, mix_turned, 2 * t + 2)
                    load_mix(t + 2, u)
                if last:
                    sp.wait_ge(mix_turned, 2 * TILES)
                    load_slabs(28, 29)
                wait(sp, x2_done, t + 1)
                sp.dma_start(acc_d[rows(t), :], o_x2).then_inc(acc_out, 16)
                if ahead(t):
                    load_ox(t + 2, u)
                wait(sp, h2_done, t + 1)
                sp.dma_start(h2_d[rows(t), :], o_h2).then_inc(h2_out, 16)

            over_tiles(sp, stage_o, before_last=lambda: load_slabs(25, 26, 27))

            def expert_step(e, slabs_of):
                for j in slabs_of:
                    w = (expert_w_gate, expert_w_up, expert_w_down)[j // 2]
                    load(expert(w, e - 1 if j > 3 else e, j % 2), *expert_slab(e, j))

            expert_step(1, range(3, 6))
            with sp.Fori(2, NE) as e:
                expert_step(e, range(6))
            for j in range(2):
                load(expert(expert_w_down, NE - 1, j), *expert_slab(NE, 4 + j))

            sp.wait_ge(over_listed, 1)
            n_over = sp.value_load(over_n[0:1, 0:1], min_val=0, max_val=MAX_OVER)
            with sp.If(n_over > 0):
                with sp.Fori(0, MAX_OVER) as item:
                    with sp.If(n_over > item):
                        e = sp.value_load(over_ei[0:1, bass.ds(item, 1)], min_val=0, max_val=NE - 1)
                        for j in range(6):
                            w = (expert_w_gate, expert_w_up, expert_w_down)[j // 2]
                            load(expert(w, e, j % 2), *over_slab(item, j))

            sp.wait_ge(moe_done, 1)
            for t in range(TILES):
                sp.dma_start(f_x[t], acc_d[t * P:(t + 1) * P, :]).then_inc(f_in[t], 16)
            for t in range(TILES):
                sp.wait_ge(f_norm, t + 1)
                sp.dma_start(out_rows[t * P:(t + 1) * P, :], f_x[t]).then_inc(f_out, 16)
            sp.wait_ge(f_out, 16 * TILES)

        @block.gpsimd
        def _(pool):
            def carry(place):
                return lambda: nc.gpsimd.tensor_tensor(scrap[:, place:place + 1], mhalf[:], mhalf[:], ALU.add)

            pool.wait_ge(raw_in[1], 16)
            pool.dma_start(m_in, masks).then_inc(mask_in, 16)
            pool.dma_start(chan[:].rearrange("p a n -> p (a n)").rearrange("p (g q) -> p g q", q=P),
                           gmlp_ws[0].rearrange("g q p -> q g p")).then_inc(ws_in, 16)
            pool.dma_start(bs[:], gmlp_bs).then_inc(small_in, 16)
            pool.dma_start(sinks[:], attn_sinks.broadcast_to([P, HEADS])).then_inc(small_in, 16)
            pool.dma_start(router_w[:, :, 0:N_GRP], router_group_w[0].rearrange("(k p) n -> p k n", p=P)).then_inc(small_in, 16)
            pool.dma_start(router_w[:, :, GPAD:], router_expert_w[0].rearrange("(k p) n -> p k n", p=P)).then_inc(small_in, 16)
            pool.dma_start(router_b[:, 0:N_GRP], router_group_b.broadcast_to([P, N_GRP])).then_inc(small_in, 16)
            pool.dma_start(router_b[:, GPAD:], router_expert_b.broadcast_to([P, NE])).then_inc(small_in, 16)

            def inverse_root(src, eps_sem, eps_count, dst, done):
                nc.gpsimd.tensor_tensor(src, src, epsc[:], ALU.add).then_inc(eps_sem, 1)
                wait(pool, eps_sem, eps_count)
                nc.gpsimd.tensor_tensor(dst, src, mhalf[:], ALU.pow).then_inc(done, 1)

            def stage_a(pair, u, first, last):
                t = 2 * pair + u
                wait_apart(pool, sq_done, t + 1, carry(0))
                inverse_root(meansq[:, u:u + 1], eps_done, t + 1, rstd[:, bass.ds(t, 1)], rstd_done)

            pool.wait_ge(mh_set, 1)
            def set_up():
                pool.wait_ge(con_in, 16)
                nc.gpsimd.tensor_copy(identb[:], con[:, C_ID:C_ID + P])
                nc.gpsimd.tensor_copy(trib[:], con[:, C_TRI:C_TRI + P])
                pool.wait_ge(mask_in, 16)
                nc.gpsimd.tensor_copy(maskb[:, :, :].rearrange("p a n -> p (a n)"), m_in[:, 0:M_CAUSAL])
                pool.wait_ge(ws_copied, 1)
                causal = m_in[:, M_CAUSAL:M_END].unsqueeze(1).broadcast_to([P, GROUPS, P])
                nc.gpsimd.tensor_tensor(wsT[:], wsT[:], causal, ALU.mult).then_inc(setup_done, 1)

            over_tiles(pool, stage_a, before_last=set_up)
            pool.wait_ge(ws_turned, 1)
            for n, v in enumerate((gmlp_ln_g, gmlp_ln_b)):
                pool.dma_start(chan[:, n, :], v.broadcast_to([P, GW])).then_inc(chan_in, 16)

            def ln_root(pair, u, first, last):
                t = 2 * pair + u
                wait_apart(pool, ln_stat, t + 1, carry(0))
                inverse_root(lnmv[:, u, 1:2], ln_eps, t + 1, lnrs[:, u:u + 1], ln_rstd)

            over_tiles(pool, ln_root)
            pool.wait_ge(ln_done, TILES)
            pool.dma_start(chan[:].rearrange("p a n -> p (a n)"), norm2_g.broadcast_to([P, D])).then_inc(g2_in, 16)

            pool.wait_ge(dve_evac, 4 * TILES)
            nc.gpsimd.memset(mone, -1.0).then_inc(w_done, 2)
            nc.gpsimd.tensor_copy(route[:, 0:NE, :, 0], con[:, C_P:C_P + 1].unsqueeze(2).broadcast_to([P, NE, TILES]))
            nc.gpsimd.tensor_copy(route[:, 0:NE, :, 1], con[:, C_TILE:C_TILE + TILES].unsqueeze(1).broadcast_to([P, NE, TILES]))

            def weights(t, u):
                G = nc.gpsimd
                wait_apart(pool, exps_done, t + 1, carry(7))
                pool.drain()
                G.tensor_tensor(wts[:, 0:1], ex[:, u], gsum[:, u], ALU.mult)
                pool.drain()
                G.tensor_tensor(wts[:, 1:2], wts[:, 0:1], gsum[:, u], ALU.add)
                pool.drain()
                G.tensor_tensor(wts[:, 2:3], wts[:, 1:2], mone, ALU.pow)
                pool.drain()
                G.tensor_tensor(wts[:, 3:4], wts[:, 2:3], ex[:, u], ALU.mult)
                G.tensor_scalar(wq[:, 0, :], con[:, C_IOTA32:C_IOTA32 + NE], eidx[:, u, 0:1], wts[:, 2:3], ALU.is_equal, ALU.mult)
                pool.drain()
                G.tensor_scalar(wq[:, 1, :], con[:, C_IOTA32:C_IOTA32 + NE], eidx[:, u, 1:2], wts[:, 3:4], ALU.is_equal, ALU.mult)
                pool.drain()
                G.tensor_tensor(wq[:, 2, :], wq[:, 0, :], wq[:, 1, :], ALU.add)
                pool.drain()

                def piece(part):
                    return route[:, 0:NE, bass.ds(t, 1), 2 + part].rearrange("p e i -> p (e i)")

                G.tensor_copy(piece(0), wq[:, 2, :])
                pool.drain()
                G.tensor_tensor(wq[:, 0, :], wq[:, 2, :], piece(0), ALU.subtract)
                pool.drain()
                G.tensor_copy(piece(1), wq[:, 0, :])
                pool.drain()
                G.tensor_tensor(wq[:, 1, :], wq[:, 0, :], piece(1), ALU.subtract)
                pool.drain()
                G.tensor_copy(piece(2), wq[:, 1, :])
                G.tensor_tensor(wts[:, 0:1], mone, mone, ALU.mult).then_inc(w_done, 1)
                pool.drain()

            def norm2_root(pair, u, first, last):
                t = 2 * pair + u
                wait_apart(pool, sq2_done, t + 1, carry(0))
                inverse_root(meansq[:, u:u + 1], eps2_done, t + 1, rstd2[:, u:u + 1], rstd2_done)
                if not (type(t) is int and t < 2):
                    weights(t - 2, u)

            over_tiles(pool, norm2_root)
            weights(TILES - 2, 0)
            weights(TILES - 1, 1)

            def one_hot(m, more=()):
                wait_apart(pool, tab_done, m, carry(1), more)
                nc.gpsimd.tensor_copy(e_pos[:], pos[:, bass.ds(m, 1), :].rearrange("p a i -> p (a i)")).then_inc(pos_copied, 1)
                wait_apart(pool, pos_copied, m - 1, carry(2))
                for i in range(TILES):
                    last = nc.gpsimd.tensor_scalar(e_hot[:, i, :], con[:, C_SLOT:C_SLOT + P], e_pos[:, i:i + 1], None, ALU.is_equal)
                last.then_inc(hot_done, 1)

            def gather(m):
                wait_apart(pool, tab_read, m + 1, carry(3), [(xs_in, 16 * m)])
                nc.gpsimd.tensor_copy(e_grow[:], e_row[:, bass.ds(m, 1)]).then_inc(row_copied, 1)
                wait_apart(pool, row_copied, m + 1, carry(4), [(xs_turned, m)])
                nc.gpsimd.indirect_dma_start(
                    out=e_xs, out_offset=None, in_=h2_d,
                    in_offset=bass.IndirectOffsetOnAxis(ap=e_grow[:, 0:1], axis=0),
                    bounds_check=SEQ - 1, oob_is_err=False).then_inc(xs_in, 16)

            def scatter(m):
                wait_apart(pool, y_out, 16 * m, carry(5))
                nc.gpsimd.tensor_copy(e_srow[:], e_row[:, bass.ds(m, 1)]).then_inc(srow_copied, 1)
                wait_apart(pool, srow_copied, m + 1, carry(6), [(y_done, m + 1)])
                nc.gpsimd.indirect_dma_start(
                    out=acc_d, out_offset=bass.IndirectOffsetOnAxis(ap=e_srow[:, 0:1], axis=0),
                    in_=e_y, in_offset=None, bounds_check=SEQ - 1, oob_is_err=False,
                    compute_op=ALU.add).then_inc(y_out, 16)

            pool.wait_ge(pos_done, 1)
            pool.wait_ge(h2_out, 16 * TILES)
            pool.wait_ge(acc_out, 16 * TILES)
            gather(0)
            gather(1)
            pool.dma_start(gf, final_norm_g.rearrange("(a n) -> a n", a=1).broadcast_to([P, D])).then_inc(gf_in, 16)

            def step(e):
                fixed = type(e) is int
                if not fixed or e + 2 < NE:
                    one_hot(e + 2)
                if not fixed or 2 <= e <= NE + 1:
                    scatter(e - 2)
                if not fixed or e + 2 < NE:
                    gather(e + 2)

            for e in range(3):
                step(e)
            with pool.Fori(3, NE - 2) as e:
                step(e)
            for e in range(NE - 2, NE + 2):
                step(e)

            pool.wait_ge(over_listed, 1)
            n_over = pool.value_load(over_n[0:1, 0:1], min_val=0, max_val=MAX_OVER)
            with pool.If(n_over > 0):
                with pool.Fori(0, MAX_OVER) as item:
                    with pool.If(n_over > item):
                        one_hot(item + NE, [(over_pos, item + 1)])
                        gather(item + NE)
                        scatter(item + NE)
                        pool.drain()
                        wait_apart(pool, y_out, (item + NE + 1) * 16, carry(0))
            pool.drain()
            pool.wait_ge(y_out, 16 * NE)

            nc.gpsimd.tensor_tensor(scrap[:, 0:1], mhalf[:], mhalf[:], ALU.add).then_inc(moe_done, 1)
            for t in range(TILES):
                pool.wait_ge(f_sq, t + 1)
                inverse_root(rstd[:, t:t + 1], f_eps, t + 1, hrstd[:, t:t + 1], f_rstd)

        @block.scalar
        def _(act):
            def carry():
                nc.scalar.activation(scrap_a[:], epsc[:], ACT.Copy)

            act.dma_start(con[:, 0:P], consts[:, 0:P]).then_inc(ident_in, 16)
            act.dma_start(g1[:], norm1_g).then_inc(g1_in, 16)
            act.wait_ge(mh_set, 1)

            def stage_half(stage, t_next, n, h):
                wait(act, half_free, n - 1)
                nc.scalar.activation(sth[:, 4 * h:4 * h + 4, :], xgt[:, 4 * h:4 * h + 4, rows(t_next)], ACT.Copy).then_inc(hi_half, 1)

            def square_a(t, u, pair):
                wait(act, x_in[u], 16 * pair + 16)
                wait(act, rstd_done, t - 1)
                wait(act, sq_done, t)
                nc.scalar.activation(a_junk, a_x[:, u, :], ACT.Square, scale=D ** -0.5,
                                     accum_out=meansq[:, u:u + 1]).then_inc(sq_done, 1)

            square_a(0, 0, 0)
            split_hi(act, 0)
            act.wait_ge(xgt_done, 1)
            for h in range(2):
                stage_half(0, 0, half_no(0, 0, h), h)
            split_hi(act, 1)
            split_hi(act, 2)

            def stage_a(pair, u, first, last):
                t = 2 * pair + u
                if not last:
                    square_a(t + 1, 1 - u, pair + u)
                    wait(act, xgt_done, t + 2)
                for h in range(2):
                    stage_half(0, 0 if last else t + 1, half_no(0, t + 1, h), h)
                wait(act, half_free, half_no(0, t, 1) + 1)
                wait(act, rstd_done, t + 1)
                wait(act, qkv_out[u], 16 * pair)
                scale = rstd[:, bass.ds(t, 1)]
                nc.scalar.activation(a_qkv[:, u, 0:512].rearrange("p (j m d) -> p m j d", m=2, d=HD),
                                     pA[u][:, 0, :].rearrange("p (m j d) -> p m j d", m=2, d=HD), ACT.Copy, scale=scale)
                nc.scalar.activation(a_qkv[:, u, 512:QKV], pA[u][:, 1, 0:256], ACT.Copy, scale=scale).then_inc(act_evac, 1)

            def copy_ws():
                split_hi(act, 4)
                act.wait_ge(ws_turned, 1)
                nc.scalar.copy(wsT[:, 0:4, :].rearrange("p g q -> p (g q)"), p6[:])
                nc.scalar.copy(wsT[:, 4:8, :].rearrange("p g q -> p (g q)"), p7[:]).then_inc(ws_copied, 1)

            over_tiles(act, stage_a, [lambda: split_hi(act, 3), copy_ws], lambda: split_hi(act, 5))

            def stage_b(pair, u, first, last):
                t = 2 * pair + u
                wait(act, qk_turned, t + 1)
                nc.scalar.copy(b_qT[:, :, :].rearrange("p j t -> p (j t)"), pX[:, 1, :]).then_inc(qT_done, 1)

                def exps(j):
                    n = 4 * t + j
                    wait(act, nmax_done, n + 1)
                    wait(act, p_turned, n - 1)
                    for m in range(KV_HEADS):
                        h = 2 * j + m
                        last_ = nc.scalar.activation(b_p[:, j % 2, 256 * m:256 * m + 256], pA[1][:, j % 2, 256 * m:256 * m + 256],
                                                     ACT.Exp, bias=nmax[:, h:h + 1], scale=HD ** -0.5, accum_out=esum[:, h:h + 1])
                    last_.then_inc(exp_done, 1)

                exps(0)
                for n in slabs_of_b(pair, u):
                    split_hi(act, n)
                exps(1)
                exps(2)
                t_next = 0 if last else t + 1
                stage_half(1, t_next, half_no(1, t + 1, 0), 0)
                exps(3)
                wait(act, sink_arg, t + 1)
                nc.scalar.activation(sinke[:], sinke[:], ACT.Exp).then_inc(sink_exp, 1)
                wait(act, zv_done, t + 1)
                wait(act, z_out[1 - u], 16 * (pair + u))
                if first:
                    act.wait_ge(qkv_out[0], 64)
                    act.wait_ge(qkv_out[1], 64)
                scale = rstd[:, bass.ds(t, 1)]
                nc.scalar.activation(b_z[:, 1, :], pA[0][:, 0, :], ACT.Copy, scale=scale).then_inc(zv_read, 1)
                stage_half(1, t_next, half_no(1, t + 1, 1), 1)
                act.drain()
                wait_apart(act, half_free, half_no(1, t, 1) + 1, carry)
                nc.scalar.activation(b_z[:, 0, :], pA[0][:, 1, :], ACT.Copy, scale=scale).then_inc(act_evac, 1)

            over_tiles(act, stage_b)

            for c_stage in range(4):
                gmlp = c_stage == 0
                base = 8 * c_stage
                half_stage = 2 + c_stage
                def gelu(t, u, pair):
                    wait(act, z_in[u], 16 * pair + 16)
                    nc.scalar.activation(c_z[u], c_z[u], ACT.Gelu_apprx_tanh).then_inc(gelu_done, 1)

                if gmlp:
                    gelu(0, 0, 0)

                def stage_c(pair, u, first, last):
                    t = 2 * pair + u
                    wait(act, src_turned, base + t + 1)
                    nc.scalar.copy(bth[:, :, :].rearrange("p k t -> p (k t)"), pX[:, 0, :]).then_inc(hi_src, 1)
                    if gmlp and first:
                        split_hi(act, 9)
                    if not (last and c_stage == 3):
                        for h in range(2):
                            stage_half(half_stage, 0 if last else t + 1, half_no(half_stage, t + 1, h), h)
                    if gmlp and not last:
                        gelu(t + 1, 1 - u, pair + u)
                    wait(act, half_free, half_no(half_stage, t, 1) + 1)
                    wait(act, gate_out[u], 64 * c_stage + 16 * pair)
                    if first and gmlp:
                        act.wait_ge(hrstd_done, 1)
                    nc.scalar.activation(c_out[:, u, :], pA[u][:, 0, :], ACT.Tanh, scale=hrstd[:, bass.ds(t, 1)]).then_inc(act_evac, 1)

                n0 = (SLAB_C0, SLAB_C1, SLAB_E0, SLAB_E1)[c_stage] + 3
                over_tiles(act, stage_c, [lambda n=n: split_hi(act, n) for n in (n0, n0 + 1)], lambda: split_hi(act, n0 + 2))

            def stage_mix(t, h):
                wait(act, mix_turned, 2 * t + h + 1)
                wait(act, half_free, half_no(6, t, h) - 1)
                nc.scalar.activation(sth[:, 4 * h:4 * h + 4, :].rearrange("p k t -> p (k t)"), pX[:, h, :], ACT.Copy, scale=0.5).then_inc(hi_half, 1)

            stage_mix(0, 0)
            stage_mix(0, 1)
            split_hi(act, 22)

            def h2T(t):
                wait(act, h2_turned, t + 1)
                wait(act, log_done, t)
                nc.scalar.copy(o_h2T[:, 0:4, :].rearrange("p k t -> p (k t)"), p6[:])
                nc.scalar.copy(o_h2T[:, 4:8, :].rearrange("p k t -> p (k t)"), p7[:]).then_inc(h2T_done, 1)

            def router_exps(t, u):
                act.drain()
                wait(act, top_done, t + 1)
                wait(act, w_done, t + 1)
                nc.scalar.activation(gexp, lg[:, u, 0:N_GRP], ACT.Exp, bias=ntop[:, u, 0:1], accum_out=gsum[:, u])
                nc.scalar.activation(ex[:, u], e8[:, u, 1:2], ACT.Exp, bias=ntop[:, u, 1:2]).then_inc(exps_done, 1)

            def stage_o(pair, u, first, last):
                t = 2 * pair + u
                if not last:
                    stage_mix(t + 1, 0)
                if not first:
                    h2T(t - 1)
                if not last:
                    stage_mix(t + 1, 1)
                wait(act, x2_done, t + 1)
                wait(act, rstd2_done, t - 1)
                wait(act, sq2_done, t)
                nc.scalar.activation(junk, o_x2, ACT.Square, scale=D ** -0.5, accum_out=meansq[:, u:u + 1]).then_inc(sq2_done, 1)
                if not (type(t) is int and t < 2):
                    router_exps(t - 2, u)

            over_tiles(act, stage_o, [lambda: split_hi(act, 23), lambda: split_hi(act, 24)])
            h2T(TILES - 1)
            split_hi(act, 25)
            router_exps(TILES - 2, 0)
            split_hi(act, 26)
            split_hi(act, 27)
            router_exps(TILES - 1, 1)
            split_hi(act, 28)

            def stage_xs(m, item=None):
                wait(act, xs_turned, m + 1)
                wait(act, slab_free, before(up_count, m, item))
                nc.scalar.copy(sth[:, 0:4, :].rearrange("p k t -> p (k t)"), pX[:, 0, :])
                nc.scalar.copy(sth[:, 4:8, :].rearrange("p k t -> p (k t)"), pX[:, 1, :]).then_inc(hi_xs, 1)

            def silu(m, item=None):
                wait(act, slab_free, gate_count(m, item))
                wait(act, hid_done, m)
                nc.scalar.activation(e_sil, pA[0][:, 0, :], ACT.Silu).then_inc(sil_done, 1)

            def stage_hid(m, item=None):
                wait(act, hid_turned, m + 1)
                wait(act, slab_free, before(down_count, m, item))
                nc.scalar.copy(bth[:, :, :].rearrange("p k t -> p (k t)"), p6[:]).then_inc(hi_hid, 1)

            def scaled_y(m, item=None):
                wait(act, slab_free, down_count(m, item))
                wait(act, y_out, 16 * m)
                nc.scalar.activation(e_y, pA[1][:, :, :].rearrange("p a n -> p (a n)"), ACT.Copy,
                                     scale=e_ws[:, bass.ds(m, 1)]).then_inc(y_done, 1)

            stage_xs(0)

            def step(e):
                fixed = type(e) is int
                if not fixed or e >= 2:
                    scaled_y(e - 2)
                if not fixed or 1 <= e < NE - 1:
                    split_hi(act, *expert_slab(e + 1, 0))
                    split_hi(act, *expert_slab(e + 1, 1))
                if fixed and e == NE - 1:
                    split_hi(act, *expert_slab(NE, 4))
                    split_hi(act, *expert_slab(NE, 5))
                if not fixed or e < NE:
                    silu(e)
                if not fixed or 1 <= e <= NE:
                    stage_hid(e - 1)
                if not fixed or e < NE - 1:
                    split_hi(act, *expert_slab(e + 1, 2))
                    split_hi(act, *expert_slab(e + 1, 3))
                    stage_xs(e + 1)
                    split_hi(act, *expert_slab(e + 1, 4))
                    split_hi(act, *expert_slab(e + 1, 5))

            for e in range(3):
                step(e)
            with act.Fori(3, NE - 2) as e:
                step(e)
            for e in range(NE - 2, NE + 2):
                step(e)

            act.wait_ge(over_listed, 1)
            n_over = act.value_load(over_n[0:1, 0:1], min_val=0, max_val=MAX_OVER)
            with act.If(n_over > 0):
                with act.Fori(0, MAX_OVER) as item:
                    with act.If(n_over > item):
                        stage_xs(item + NE, item)
                        for j in range(6):
                            split_hi(act, *over_slab(item, j))
                        silu(item + NE, item)
                        stage_hid(item + NE, item)
                        scaled_y(item + NE, item)

            for t in range(TILES):
                act.wait_ge(f_in[t], 16)
                wait(act, f_sq, t)
                nc.scalar.activation(junk, f_x[t], ACT.Square, scale=D ** -0.5, accum_out=rstd[:, t:t + 1]).then_inc(f_sq, 1)

        @block.vector
        def _(dve):
            V = nc.vector
            V.memset(epsc[:], EPS)
            V.memset(mhalf[:], -0.5).then_inc(mh_set, 1)
            V.memset(onesb[:], 1.0)
            V.memset(b_v[:, 1, :], 0.0)
            V.memset(router_w[:, :, N_GRP:GPAD], 0.0)
            V.memset(router_b[:, N_GRP:GPAD], NEG)

            def x_to_sbuf(t):
                wait(dve, x_turned, t + 1)
                V.tensor_tensor(xgt[:, :, rows(t)], pX[:, :, :].rearrange("p a (k t) -> p (a k) t", t=P),
                                g1[:].unsqueeze(2).broadcast_to([P, KT, P]), ALU.mult).then_inc(xgt_done, 1)

            def stage_half(t_next, n, h):
                wait(dve, hi_half, n + 1)
                wait(dve, half_free, n - 1)
                V.tensor_sub(stl[:, 4 * h:4 * h + 4, :], xgt[:, 4 * h:4 * h + 4, rows(t_next)],
                             sth[:, 4 * h:4 * h + 4, :].bitcast(F32)).then_inc(lo_half, 1)

            dve.wait_ge(g1_in, 16)
            x_to_sbuf(0)
            split_lo(dve, 0)
            dve.wait_ge(xgt_done, 1)
            for h in range(2):
                stage_half(0, half_no(0, 0, h), h)
            split_lo(dve, 1)
            split_lo(dve, 2)
            def stage_a(pair, u, first, last):
                t = 2 * pair + u
                if not last:
                    x_to_sbuf(t + 1)
                    wait(dve, xgt_done, t + 2)
                for h in range(2):
                    stage_half(0 if last else t + 1, half_no(0, t + 1, h), h)
                wait(dve, act_evac, t + 1)
                heads = a_qkv[:, u, 0:640].rearrange("p (h d) -> p h d", d=HD)
                prod = a_rot[:, 0, :].rearrange("p (h d) -> p h d", d=ROT)
                turn = a_rot[:, 1, :].rearrange("p (h d) -> p h d", d=ROT)

                def table(c0, lo, n):
                    return con[:, bass.ds(t * ROT + c0 + lo, n)].unsqueeze(1).broadcast_to([P, 10, n])

                if first:
                    dve.wait_ge(con_in, 16)
                wait(dve, rope_done, t)
                V.tensor_tensor(prod, heads[:, :, 0:ROT], table(C_COS, 0, ROT), ALU.mult)
                V.tensor_tensor(turn[:, :, 0:8], heads[:, :, 8:16], table(C_SIN, 0, 8), ALU.mult)
                V.tensor_tensor(turn[:, :, 8:16], heads[:, :, 0:8], table(C_SIN, 8, 8), ALU.mult)
                dve.drain()
                V.tensor_tensor(heads[:, :, 0:ROT], prod, turn, ALU.add).then_inc(rope_done, 1)

            over_tiles(dve, stage_a, [lambda: split_lo(dve, 3), lambda: split_lo(dve, 4)], lambda: split_lo(dve, 5))

            dve.wait_ge(small_in, 16 * 6)
            V.tensor_scalar(nsinks[:], sinks[:], -1.0, None, ALU.mult)
            dve.wait_ge(rstd_done, TILES)
            V.tensor_scalar(hrstd[:], rstd[:], 0.5, None, ALU.mult).then_inc(hrstd_done, 1)
            V.memset(b_kT, 0.0)
            dve.drain()

            def stage_b(pair, u, first, last):
                t = 2 * pair + u
                wait(dve, qkv_in[u], 16 * pair + 16)
                wait(dve, qk_turned, t + 1)
                V.tensor_copy(b_v[:, u, :], b_qkv[:, u, 640:QKV])
                for m in range(KV_HEADS):
                    last_ = V.tensor_copy(b_kT[64 * m:64 * m + 64, m, u * P:u * P + P], pX[64 * m:64 * m + 64, 0, 0:P])
                dve.drain()
                V.tensor_copy(lnst[:, 0:1], mhalf[:]).then_inc(kT_done, 1)

                def maxima(j):
                    n = 4 * t + j
                    wait(dve, s_done, n + 1)
                    V.reduce_max(nmax[:, 2 * j:2 * j + 2], pA[1][:, j % 2, :].rearrange("p (m k) -> p m k", m=2), AX_X)
                    dve.drain()
                    V.scalar_tensor_tensor(out=nmax[:, 2 * j:2 * j + 2], in0=nmax[:, 2 * j:2 * j + 2], scalar=-(HD ** -0.5),
                                           in1=nsinks[:, 2 * j:2 * j + 2], op0=ALU.mult, op1=ALU.min).then_inc(nmax_done, 1)

                def keep_pT(j):
                    wait(dve, p_turned, 4 * t + j + 1)
                    wait(dve, pv_done, 4 * t + j - 1)
                    if first and j == 1:
                        dve.wait_ge(qkv_out[0], 64)
                    V.tensor_copy(b_pT[:, j % 2, :], (p6, p7)[j % 2][:]).then_inc(pT_done, 1)

                maxima(0)
                maxima(1)
                for n in slabs_of_b(pair, u):
                    split_lo(dve, n)
                keep_pT(0)
                maxima(2)
                keep_pT(1)
                t_next = 0 if last else t + 1
                stage_half(t_next, half_no(1, t + 1, 0), 0)
                maxima(3)
                dve.wait_ge(nmax_done, 4 * t + 4)
                V.tensor_tensor(sinke[:], sinks[:], nmax[:], ALU.add).then_inc(sink_arg, 1)
                keep_pT(2)
                wait(dve, sink_exp, t + 1)
                wait(dve, exp_done, 4 * t + 4)
                V.tensor_tensor(rden[:], esum[:], sinke[:], ALU.add)
                dve.drain()
                V.reciprocal(rden[:], rden[:])
                keep_pT(3)
                stage_half(t_next, half_no(1, t + 1, 1), 1)
                wait(dve, pv_done, 4 * t + 4)
                wait(dve, ao_out[1 - u], 16 * (pair + u))
                V.tensor_tensor(b_out[:].rearrange("p (m j d) -> p m j d", m=2, d=HD),
                                pX[:, 0, :].rearrange("p (m j d) -> p m j d", m=2, d=HD),
                                rden[:].rearrange("p (j m) -> p m j", m=2).unsqueeze(3).broadcast_to([P, 2, PAIRS, HD]),
                                ALU.mult).then_inc(o_done, 1)

            over_tiles(dve, stage_b)

            for c_stage in range(4):
                gmlp, adds = c_stage == 0, c_stage >= 2
                base = 8 * c_stage
                half_stage = 2 + c_stage

                def ln_stats(t, u):
                    wait(dve, gelu_done, t + 1)
                    V.bn_stats(lnst[:], c_z[u][:, GW:2 * GW])
                    dve.drain()
                    V.bn_aggr(lnmv[:, u, :], lnst[:]).then_inc(ln_stat, 1)

                def ln_apply(t, u):
                    v = c_z[u][:, GW:2 * GW]
                    wait(dve, ln_rstd, t + 1)
                    V.tensor_scalar(v, v, lnmv[:, u, 0:1], lnrs[:, u:u + 1], ALU.subtract, ALU.mult)
                    dve.drain()
                    V.tensor_tensor(v, v, chan[:, 0, :], ALU.mult)
                    dve.drain()
                    V.tensor_tensor(v, v, chan[:, 1, :], ALU.add).then_inc(ln_done, 1)

                if gmlp:
                    dve.wait_ge(chan_in, 32)
                    ln_stats(0, 0)
                    ln_apply(0, 0)

                def stage_c(pair, u, first, last):
                    t = 2 * pair + u
                    wait(dve, hi_src, base + t + 1)
                    V.tensor_sub(btl[:, :, :].rearrange("p k t -> p (k t)"), pX[:, 0, :],
                                 bth[:, :, :].rearrange("p k t -> p (k t)").bitcast(F32)).then_inc(lo_src, 1)
                    if gmlp and first:
                        split_lo(dve, 9)
                    staged = not (last and c_stage == 3)
                    if staged:
                        stage_half(0 if last else t + 1, half_no(half_stage, t + 1, 0), 0)
                    if staged:
                        stage_half(0 if last else t + 1, half_no(half_stage, t + 1, 1), 1)
                    if gmlp:
                        wait(dve, mix_done, t + 1)
                        v = c_z[u][:, GW:2 * GW]
                        V.tensor_tensor(v.rearrange("p (g d) -> p g d", g=GROUPS), p6[:].rearrange("p (g d) -> p g d", g=GROUPS),
                                        bs[:].unsqueeze(2).broadcast_to([P, GROUPS, GW // GROUPS]), ALU.add)
                        dve.drain()
                        if first:
                            dve.wait_ge(z_out[0], 64)
                            dve.wait_ge(z_out[1], 64)
                        wait(dve, g_out[u], 16 * pair)
                        V.tensor_tensor(c_g[:, u, :], c_z[u][:, 0:GW], v, ALU.mult).then_inc(g_done, 1)
                    if gmlp and not last:
                        ln_stats(t + 1, 1 - u)
                        ln_apply(t + 1, 1 - u)
                    wait(dve, tile_done, base + t + 1)
                    wait(dve, act_evac, 2 * TILES + base + t + 1)
                    gated = V.scalar_tensor_tensor(out=c_out[:, u, :], in0=c_out[:, u, :], scalar=1.0, in1=pA[u][:, 1, :],
                                                   op0=ALU.add, op1=ALU.mult)
                    if adds:
                        dve.drain()
                        wait(dve, am_in[u], 64 * (c_stage - 2) + 16 * pair + 16)
                        gated = V.tensor_tensor(c_out[:, u, :], c_out[:, u, :], c_z[u][:, 0:HALF], ALU.add)
                    gated.then_inc(dve_evac, 1)

                n0 = (SLAB_C0, SLAB_C1, SLAB_E0, SLAB_E1)[c_stage] + 3
                over_tiles(dve, stage_c, [lambda n=n: split_lo(dve, n) for n in (n0, n0 + 1)], lambda: split_lo(dve, n0 + 2))

            def stage_mix(t, h):
                wait(dve, hi_half, half_no(6, t, h) + 1)
                V.scalar_tensor_tensor(out=stl[:, 4 * h:4 * h + 4, :].rearrange("p k t -> p (k t)"), in0=pX[:, h, :], scalar=0.5,
                                       in1=sth[:, 4 * h:4 * h + 4, :].rearrange("p k t -> p (k t)").bitcast(F32),
                                       op0=ALU.mult, op1=ALU.subtract).then_inc(lo_half, 1)

            stage_mix(0, 0)
            stage_mix(0, 1)
            split_lo(dve, 22)
            dve.wait_ge(g2_in, 16)
            V.memset(csum[:, 0, :], 0.0)
            V.memset(over_n[:], 0.0)

            def then(_):
                dve.drain()

            def keep_logits(t, u):
                wait(dve, log_done, t + 1)
                wait(dve, w_done, t + 1)
                V.tensor_tensor(lg[:, u, :], p6[:, 0:LOGITS], router_b[:], ALU.add).then_inc(log_read, 1)

            def choose(t, u):
                iota = con[:, C_IOTA32:C_IOTA32 + NE]
                dve.drain()
                then(V.max(g8, lg[:, u, 0:GPAD]))
                V.tensor_scalar(ntop[:, u, 0:1], g8[:, 0:1], -1.0, None, ALU.mult)
                then(V.max_index(gi8, g8, lg[:, u, 0:GPAD]))
                then(V.tensor_copy(gidx, gi8[:, 0:1]))
                then(V.tensor_scalar(gmask, con[:, C_GROUP:C_GROUP + NE], gidx, NEG, ALU.not_equal, ALU.mult))
                then(V.tensor_tensor(ev, lg[:, u, GPAD:LOGITS], gmask, ALU.add))
                then(V.max(e8[:, u, :], ev))
                V.tensor_scalar(ntop[:, u, 1:2], e8[:, u, 0:1], -1.0, None, ALU.mult)
                then(V.max_index(ei8, e8[:, u, :], ev))
                V.tensor_copy(eidx[:, u, :], ei8[:, 0:2]).then_inc(top_done, 1)
                wait(dve, top_done, t + 1)
                then(V.tensor_scalar(hot1, iota, eidx[:, u, 0:1], None, ALU.is_equal))
                now = chosen[:, bass.ds(t, 1), :].rearrange("p a e -> p (a e)")
                then(V.scalar_tensor_tensor(out=now, in0=iota, scalar=eidx[:, u, 1:2], in1=hot1, op0=ALU.is_equal, op1=ALU.add))
                then(V.tensor_tensor(csum[:, bass.ds(t + 1, 1), :].rearrange("p a e -> p (a e)"),
                                     csum[:, bass.ds(t, 1), :].rearrange("p a e -> p (a e)"), now, ALU.add))

            def stage_o(pair, u, first, last):
                t = 2 * pair + u
                if not last:
                    stage_mix(t + 1, 0)
                    stage_mix(t + 1, 1)
                wait(dve, half_free, half_no(6, t, 1) + 1)
                wait(dve, ox_in[u], 16 * pair + 16)
                wait(dve, acc_out, 16 * t)
                V.tensor_tensor(o_x2, pA[u][:, :, :].rearrange("p a n -> p (a n)"), o_x[u], ALU.add).then_inc(x2_done, 1)
                if not first:
                    keep_logits(t - 1, 1 - u)
                if last:
                    wait(dve, x2_done, t + 1)
                    V.memset(e_xs, 0.0)
                wait(dve, x2_done, t + 1)
                wait(dve, rstd2_done, t + 1)
                wait(dve, h2_out, 16 * t)
                wait(dve, h2_turned, t)
                V.scalar_tensor_tensor(out=o_h2, in0=o_x2, scalar=rstd2[:, u:u + 1],
                                       in1=chan[:, :, :].rearrange("p a n -> p (a n)"),
                                       op0=ALU.mult, op1=ALU.mult).then_inc(h2_done, 1)
                if not first:
                    choose(t - 1, 1 - u)

            over_tiles(dve, stage_o, [lambda: split_lo(dve, 23), lambda: split_lo(dve, 24)])
            split_lo(dve, 25)
            keep_logits(TILES - 1, 1)
            choose(TILES - 1, 1)
            V.tensor_copy(e_tab[:], mhalf[:].broadcast_to([P, 5])).then_inc(route_set, 1)
            dve.wait_ge(ranks_done, 1)
            V.tensor_copy(count, p6[:, TILES * NE:(TILES + 1) * NE])
            dve.wait_ge(acc_out, 16 * TILES)
            then(V.scalar_tensor_tensor(out=pos[:, 0:NE, :].rearrange("p e i -> p i e"),
                                        in0=p6[:, 0:TILES * NE].rearrange("p (i e) -> p i e", e=NE), scalar=1.0, in1=chosen,
                                        op0=ALU.add, op1=ALU.mult))

            def first_hots(m):
                wait(dve, tab_done, m)
                for i in range(TILES):
                    last_ = V.tensor_scalar(e_hot[:, i, :], con[:, C_SLOT:C_SLOT + P], pos[:, m, i:i + 1], None, ALU.is_equal)
                last_.then_inc(hot_done, 1)

            first_hots(0)
            V.memset(small, 0.0).then_inc(pos_done, 1)

            def count_tiles():
                then(V.memset(over, 0.0))
                for n in range(1, TILES):
                    then(V.scalar_tensor_tensor(out=over, in0=count, scalar=n * P + 0.5, in1=over, op0=ALU.is_gt, op1=ALU.add))
                then(V.tensor_copy(ends, over))

            def sum_tiles():
                for n in (1, 2, 4, 8, 16):
                    then(V.tensor_copy(other, ends))
                    then(V.tensor_tensor(ends[:, n:NE], other[:, n:NE], other[:, 0:NE - n], ALU.add))
                then(V.tensor_copy(over_n[:], ends[:, NE - 1:NE]))

            def list_items():
                ends_bc = ends.unsqueeze(1).broadcast_to([P, MAX_OVER + 1, NE])
                numbers = con[:, C_J:C_J + MAX_OVER + 1]
                then(V.tensor_tensor(passed, ends_bc, numbers.unsqueeze(2).broadcast_to([P, MAX_OVER + 1, NE]), ALU.is_le))
                then(V.tensor_reduce(over_e[:], passed, AX_X, ALU.add))
                then(V.tensor_scalar(over_ei[:], over_e[:], float(NE - 1), None, ALU.min))
                then(V.tensor_tensor(passed, passed, ends_bc, ALU.mult))
                then(V.tensor_reduce(over_shift[:], passed, AX_X, ALU.max))
                then(V.tensor_tensor(over_shift[:], numbers, over_shift[:], ALU.subtract))
                V.tensor_scalar(over_shift[:], over_shift[:], 1.0, float(P), ALU.add, ALU.mult).then_inc(over_listed, 1)

            def tables(m):
                wait(dve, tab_done, m + 1)
                V.tensor_copy(e_tab[:], p7[:, 0:5])
                dve.drain()
                V.scalar_tensor_tensor(out=e_row[:, bass.ds(m, 1)], in0=e_tab[:, 0:1], scalar=float(FAR), in1=e_tab[:, 1:2],
                                       op0=ALU.add, op1=ALU.add)
                V.tensor_reduce(e_ws[:, bass.ds(m, 1)], e_tab[:, 2:5], AX_X, ALU.add)
                dve.drain()
                V.tensor_copy(e_tab[:, 0:1], mhalf[:]).then_inc(tab_read, 1)

            def stage_xs(m, item=None):
                wait(dve, hi_xs, m + 1)
                V.tensor_sub(stl[:, :, :].rearrange("p k t -> p (k t)"), pX[:, :, :].rearrange("p a n -> p (a n)"),
                             sth[:, :, :].rearrange("p k t -> p (k t)").bitcast(F32)).then_inc(lo_xs, 1)

            def hidden(m, item=None):
                wait(dve, slab_free, up_count(m, item))
                wait(dve, sil_done, m + 1)
                wait(dve, hid_turned, m)
                V.tensor_tensor(e_hid, e_sil, pA[0][:, 1, :], ALU.mult).then_inc(hid_done, 1)

            def stage_hid(m, item=None):
                wait(dve, hi_hid, m + 1)
                V.tensor_sub(btl[:, :, :].rearrange("p k t -> p (k t)"), p6[:],
                             bth[:, :, :].rearrange("p k t -> p (k t)").bitcast(F32)).then_inc(lo_hid, 1)

            tables(0)
            first_hots(1)
            tables(1)
            split_lo(dve, 26)
            split_lo(dve, 27)
            stage_xs(0)
            split_lo(dve, 28)

            def step(e):
                fixed = type(e) is int
                if not fixed or 1 <= e < NE - 1:
                    split_lo(dve, *expert_slab(e + 1, 0))
                    split_lo(dve, *expert_slab(e + 1, 1))
                if fixed and e == NE - 1:
                    split_lo(dve, *expert_slab(NE, 4))
                    split_lo(dve, *expert_slab(NE, 5))
                if not fixed or 1 <= e <= NE:
                    stage_hid(e - 1)
                if not fixed or e < NE - 1:
                    split_lo(dve, *expert_slab(e + 1, 2))
                    split_lo(dve, *expert_slab(e + 1, 3))
                if not fixed or e < NE:
                    hidden(e)
                if not fixed or e < NE - 1:
                    stage_xs(e + 1)
                if not fixed or e + 2 < NE:
                    tables(e + 2)
                if not fixed or e < NE - 1:
                    split_lo(dve, *expert_slab(e + 1, 4))
                    split_lo(dve, *expert_slab(e + 1, 5))

            for e, work in enumerate((count_tiles, sum_tiles, list_items)):
                step(e)
                work()
            with dve.Fori(3, NE - 2) as e:
                step(e)
            for e in range(NE - 2, NE + 1):
                step(e)

            dve.wait_ge(over_listed, 1)
            n_over = dve.value_load(over_n[0:1, 0:1], min_val=0, max_val=MAX_OVER)
            picked = area(late, 0, TILES * 5 * NE // 2).bitcast(BF16).rearrange("p (i e) -> p i e", e=NE)
            ppicked = area(late, 640, TILES, NE)
            with dve.If(n_over > 0):
                with dve.Fori(0, MAX_OVER) as item:
                    with dve.If(n_over > item):
                        then(V.tensor_scalar(o_sel[:], con[:, C_IOTA32:C_IOTA32 + NE], over_e[:, bass.ds(item, 1)], None, ALU.is_equal))
                        V.tensor_tensor(picked, route[:, 0:NE, :, :].rearrange("p e i c -> p (i c) e"),
                                        o_sel[:].unsqueeze(1).broadcast_to([P, TILES * 5, NE]), ALU.mult)
                        then(V.tensor_tensor(ppicked, pos[:, 0:NE, :].rearrange("p e i -> p i e"),
                                             o_sel[:].unsqueeze(1).broadcast_to([P, TILES, NE]), ALU.mult))
                        V.tensor_reduce(small[:, 0:TILES * 5], picked, AX_X, ALU.add)
                        then(V.tensor_reduce(small[:, TILES * 5:TILES * 6], ppicked, AX_X, ALU.add))
                        V.tensor_copy(route[:, bass.ds(item + NE, 1), :, :].rearrange("p a i c -> p (a i c)"),
                                      small[:, 0:TILES * 5])
                        then(V.tensor_scalar(pos[:, bass.ds(item + NE, 1), :].rearrange("p a i -> p (a i)"),
                                             small[:, TILES * 5:TILES * 6],
                                             over_shift[:, bass.ds(item, 1)], None, ALU.subtract))
                        V.tensor_copy(e_tab[:, 0:1], mhalf[:]).then_inc(over_pos, 1)
                        tables(item + NE)
                        stage_xs(item + NE, item)
                        for j in range(6):
                            split_lo(dve, *over_slab(item, j))
                        hidden(item + NE, item)
                        stage_hid(item + NE, item)

            dve.wait_ge(gf_in, 16)

            for t in range(TILES):
                dve.wait_ge(f_rstd, t + 1)
                V.scalar_tensor_tensor(out=f_x[t], in0=f_x[t], scalar=hrstd[:, t:t + 1], in1=gf,
                                       op0=ALU.mult, op1=ALU.mult).then_inc(f_norm, 1)

        @block.tensor
        def _(pe):
            T = nc.tensor

            def turn_x(t, u, pair):
                wait(pe, x_in[u], 16 * pair + 16)
                wait(pe, xgt_done, t)
                for k in range(KT):
                    last_ = T.transpose(pX[:, k // 4, (k % 4) * P:(k % 4) * P + P], a_x[:, u, k * P:(k + 1) * P], ident)
                last_.then_inc(x_turned, 1)

            def half_ready(n):
                wait(pe, hi_half, n + 1)
                wait(pe, lo_half, n + 1)

            pe.wait_ge(ident_in, 16)
            turn_x(0, 0, 0)
            def stage_a(pair, u, first, last):
                t = 2 * pair + u
                wait(pe, act_evac, t - 1)
                for h in range(2):
                    half_ready(half_no(0, t, h))
                    slab_ready(pe, SLAB_A + 2 * h)
                    for k in range(4 * h, 4 * h + 4):
                        last_ = product(pA[u][:, 0, :], sth, stl, SLAB_A + 2 * h, 0, (HALF, HALF), k, k % 4, k == 0, k == KT - 1)
                    if last and h == 0:
                        last_.then_inc(slab_free, 1)
                    slab_ready(pe, SLAB_A + 1)
                    for k in range(4 * h, 4 * h + 4):
                        last_ = product(pA[u][:, 1, 0:256], sth, stl, SLAB_A + 1, 0, (256, 256), k, k, k == 0, k == KT - 1)
                    last_.then_inc(half_free, 1)
                    if h == 0 and not last:
                        turn_x(t + 1, 1 - u, pair + u)
                if last:
                    pe.drain().then_inc(slab_free, 2)

            def turn_ws():
                pe.wait_ge(ws_in, 16)
                for g in range(GROUPS):
                    last_ = T.transpose((p6, p7)[g // 4][:, (g % 4) * P:(g % 4) * P + P],
                                        chan[:].rearrange("p a n -> p (a n)")[:, g * P:(g + 1) * P], ident)
                last_.then_inc(ws_turned, 1)

            over_tiles(pe, stage_a, [turn_ws])

            def stage_b(pair, u, first, last):
                t = 2 * pair + u
                if first:
                    pe.wait_ge(act_evac, TILES)

                def z_part(n):
                    h, which, sub = n // 4, (n // 2) % 2, n % 2
                    slab = SLAB_B + 2 * h + which
                    if n % 4 == 0:
                        half_ready(half_no(1, t, h))
                    if n == 0:
                        wait(pe, zv_read, t)
                    if n == 2:
                        wait(pe, act_evac, TILES + t)
                    slab_ready(pe, slab)
                    for k in range(4 * h + 2 * sub, 4 * h + 2 * sub + 2):
                        last_ = product(pA[0][:, which, :], sth, stl, slab, 0, (HALF, HALF), k, k % 4, k == 0, k == KT - 1)
                    if n == 3:
                        last_.then_inc(half_free, 1)
                    if n == 5:
                        last_.then_inc(zv_done, 1)
                    if n == 7:
                        last_.then_inc(half_free, 1)
                    if last and n == 1:
                        last_.then_inc(slab_free, 1)
                    elif last and sub == 1:
                        pe.drain().then_inc(slab_free, 1)

                def scores(j):
                    n = 4 * t + j
                    wait(pe, exp_done, n - 1)
                    s = pA[1][:, j % 2, :]
                    m = maskb[:, 4:5, :] if u else maskb[:, bass.ds(pair, 1), :]
                    T.matmul(s, identb[:], m.broadcast_to([P, 2, 256]), start=True, stop=False)
                    T.matmul(s, b_qT[:, j, :], b_kT[:, :, :].rearrange("p m k -> p (m k)"), start=False, stop=True).then_inc(s_done, 1)

                def turn_p(j):
                    n = 4 * t + j
                    wait(pe, exp_done, n + 1)
                    wait(pe, pT_done, n - 1)
                    for q in range(4):
                        last_ = T.transpose((p6, p7)[j % 2][:, q * P:(q + 1) * P], b_p[:, j % 2, q * P:(q + 1) * P], ident)
                    last_.then_inc(p_turned, 1)

                def values(j):
                    wait(pe, pT_done, 4 * t + j + 1)
                    for m in range(KV_HEADS):
                        h = m * PAIRS + j
                        for slot in range(2):
                            q = 2 * m + slot
                            last_ = T.matmul(pX[:, 0, h * HD:(h + 1) * HD], b_pT[:, j % 2, q * P:(q + 1) * P],
                                             b_v[:, slot, m * HD:(m + 1) * HD], start=(slot == 0), stop=(slot == 1))
                    last_.then_inc(pv_done, 1)

                def turn_qk():
                    wait(pe, qkv_in[u], 16 * pair + 16)
                    if first:
                        pe.wait_ge(xgt_done, TILES)
                    for j in range(PAIRS):
                        T.transpose(pX[:, 1, j * P:(j + 1) * P], b_qkv[:, u, j * P:(j + 1) * P], ident)
                    wait(pe, o_done, t)
                    T.transpose(pX[:, 0, 0:P], b_qkv[:, u, 512:640], ident).then_inc(qk_turned, 1)

                z_part(0)
                turn_qk()
                z_part(1)
                wait(pe, qT_done, t + 1)
                wait(pe, kT_done, t + 1)
                if first:
                    pe.wait_ge(setup_done, 1)
                scores(0)
                scores(1)
                z_part(2)
                z_part(3)
                turn_p(0)
                scores(2)
                z_part(4)
                turn_p(1)
                values(0)
                scores(3)
                z_part(5)
                turn_p(2)
                values(1)
                z_part(6)
                turn_p(3)
                values(2)
                z_part(7)
                values(3)

            over_tiles(pe, stage_b)

            for c_stage in range(4):
                gmlp = c_stage == 0
                base = 8 * c_stage
                slab0 = (SLAB_C0, SLAB_C1, SLAB_E0, SLAB_E1)[c_stage]
                half_stage = 2 + c_stage
                if gmlp:
                    pe.wait_ge(act_evac, 2 * TILES)
                    pe.wait_ge(exp_done, 4 * TILES)
                    pe.wait_ge(o_done, TILES)

                def stage_c(pair, u, first, last):
                    t = 2 * pair + u
                    wait(pe, act_evac, 2 * TILES + base + t - 1)
                    wait(pe, dve_evac, base + t - 1)
                    for h in range(2):
                        half_ready(half_no(half_stage, t, h))
                        slab_ready(pe, slab0 + h)
                        for k in range(4 * h, 4 * h + 4):
                            last_ = product(pA[u][:, 0, :], sth, stl, slab0 + h, 0, (HALF, HALF), k, k % 4, k == 0, k == KT - 1)
                        last_.then_inc(half_free, 1)
                        if h == 0:
                            wait(pe, src_in[u], 64 * c_stage + 16 * pair + 16)
                            wait(pe, lo_src, base + t)
                            for k in range(4):
                                last_ = T.transpose(pX[:, 0, k * P:(k + 1) * P], c_src[u][:, k * P:(k + 1) * P], ident)
                            last_.then_inc(src_turned, 1)
                    if last:
                        pe.drain().then_inc(slab_free, 2)
                    if gmlp:
                        wait(pe, ln_done, t + 1)
                        wait(pe, g_done, t)
                        for g in range(GROUPS):
                            lo = g * (GW // GROUPS)
                            last_ = T.matmul(p6[:, lo:lo + 64], wsT[:, g, :], c_z[u][:, GW + lo:GW + lo + 64], start=True, stop=True)
                        last_.then_inc(mix_done, 1)
                    slab_ready(pe, slab0 + 2)
                    wait(pe, hi_src, base + t + 1)
                    wait(pe, lo_src, base + t + 1)
                    for k in range(4):
                        last_ = product(pA[u][:, 1, :], bth, btl, slab0 + 2, 0, (HALF, HALF), k, k, k == 0, k == 3)
                    last_.then_inc(tile_done, 1)
                    if last:
                        pe.drain().then_inc(slab_free, 1)

                over_tiles(pe, stage_c)

            def turn_mix(t, u, pair, h):
                wait(pe, mix_in[u], 16 * pair + 16)
                wait(pe, lo_half, half_no(6, t, h) - 1)
                for k in range(4):
                    c0 = (4 * h + k) * P
                    last_ = T.transpose(pX[:, h, k * P:(k + 1) * P], o_mix[:, u, c0:c0 + P], ident)
                last_.then_inc(mix_turned, 1)

            pe.wait_ge(lo_src, 4 * TILES)
            turn_mix(0, 0, 0, 0)
            turn_mix(0, 0, 0, 1)

            def turn_h2(t):
                wait(pe, h2_done, t + 1)
                wait(pe, log_read, t)
                for k in range(KT):
                    last_ = T.transpose((p6, p7)[k // 4][:, (k % 4) * P:(k % 4) * P + P], o_h2[:, k * P:(k + 1) * P], ident)
                last_.then_inc(h2_turned, 1)

            def router(t):
                wait(pe, h2T_done, t + 1)
                for k in range(KT):
                    last_ = T.matmul(p6[:, 0:LOGITS], o_h2T[:, k, :], router_w[:, k, :], start=(k == 0), stop=(k == KT - 1))
                last_.then_inc(log_done, 1)

            def stage_o(pair, u, first, last):
                t = 2 * pair + u
                wait(pe, dve_evac, 4 * TILES)
                wait(pe, x2_done, t - 1)
                for h in range(2):
                    half_ready(half_no(6, t, h))
                    for c in range(2):
                        slab = SLAB_O + 2 * h + c
                        slab_ready(pe, slab)
                        for k in range(4 * h, 4 * h + 4):
                            last_ = product(pA[u][:, c, :], sth, stl, slab, 0, (HALF, HALF), k, k % 4, k == 0, k == KT - 1)
                        if last and c == 0:
                            last_.then_inc(slab_free, 1)
                    last_.then_inc(half_free, 1)
                    if not last:
                        turn_mix(t + 1, 1 - u, pair + u, h)
                    if h == 0 and not first:
                        turn_h2(t - 1)
                    if last:
                        pe.drain().then_inc(slab_free, 1)
                if not first:
                    router(t - 1)

            over_tiles(pe, stage_o)
            turn_h2(TILES - 1)
            router(TILES - 1)

            pe.wait_ge(route_set, 1)
            pe.wait_ge(log_read, TILES)
            T.matmul(p6[:, 0:TILES * NE], trib[:], chosen, start=True, stop=False)
            T.matmul(p6[:, 0:TILES * NE], onesb[:], csum[:, 0:TILES, :], start=False, stop=True)
            T.matmul(p6[:, TILES * NE:(TILES + 1) * NE], onesb[:], csum[:, TILES, :], start=True, stop=True).then_inc(ranks_done, 1)
            pe.wait_ge(pos_done, 1)
            pe.wait_ge(w_done, TILES + 2)

            def table(m):
                wait(pe, hot_done, m + 1)
                wait(pe, tab_read, m)
                for i in range(TILES):
                    rhs = route[:, bass.ds(m, 1), i, :].rearrange("p a c -> p (a c)")
                    last_ = T.matmul(p7[:, 0:5], e_hot[:, i, :], rhs, start=(i == 0), stop=(i == TILES - 1))
                last_.then_inc(tab_done, 1)

            def turn_xs(m):
                wait(pe, xs_in, m * 16 + 16)
                wait(pe, lo_xs, m)
                for k in range(KT):
                    last_ = T.transpose(pX[:, k // 4, (k % 4) * P:(k % 4) * P + P], e_xs[:, k * P:(k + 1) * P], ident)
                last_.then_inc(xs_turned, 1)

            def gate_or_up(m, c, slab_of):
                for h in range(2):
                    base, times = slab_of(2 * c + h)
                    slab_ready(pe, base, times)
                    for k in range(4 * h, 4 * h + 4):
                        last_ = product(pA[0][:, c, :], sth, stl, base, 0, (HALF, HALF), k, k % 4, k == 0, k == KT - 1)
                    last_.then_inc(slab_free, 1)

            def turn_hid(m):
                wait(pe, hid_done, m + 1)
                wait(pe, lo_hid, m)
                for k in range(4):
                    last_ = T.transpose(p6[:, k * P:(k + 1) * P], e_hid[:, k * P:(k + 1) * P], ident)
                last_.then_inc(hid_turned, 1)

            def down(m, slab_of):
                wait(pe, hi_hid, m + 1)
                wait(pe, lo_hid, m + 1)
                wait(pe, y_done, m)
                for h in range(2):
                    base, times = slab_of(4 + h)
                    slab_ready(pe, base, times)
                    for k in range(2 * h, 2 * h + 2):
                        for c in range(2):
                            last_ = product(pA[1][:, c, :], bth, btl, base, c * HALF, (D, HALF), k, k % 2, k == 0, k == 3)
                    last_.then_inc(slab_free, 1)

            table(0)
            table(1)
            turn_xs(0)

            def step(e):
                fixed = type(e) is int

                def slab_of(j):
                    return expert_slab(e, j)

                if not fixed or e < NE:
                    wait(pe, hi_xs, e + 1)
                    wait(pe, lo_xs, e + 1)
                    wait(pe, sil_done, e)
                    gate_or_up(e, 0, slab_of)
                if not fixed or 1 <= e <= NE:
                    turn_hid(e - 1)
                if not fixed or e < NE:
                    gate_or_up(e, 1, slab_of)
                if not fixed or e < NE - 1:
                    turn_xs(e + 1)
                if not fixed or e + 2 < NE:
                    table(e + 2)
                if not fixed or 1 <= e <= NE:
                    down(e - 1, slab_of)

            for e in range(3):
                step(e)
            with pe.Fori(3, NE - 2) as e:
                step(e)
            for e in range(NE - 2, NE + 1):
                step(e)

            pe.wait_ge(over_listed, 1)
            n_over = pe.value_load(over_n[0:1, 0:1], min_val=0, max_val=MAX_OVER)
            with pe.If(n_over > 0):
                with pe.Fori(0, MAX_OVER) as item:
                    with pe.If(n_over > item):
                        m = item + NE

                        def slab_of(j):
                            return over_slab(item, j)

                        table(m)
                        turn_xs(m)
                        wait(pe, hi_xs, m + 1)
                        wait(pe, lo_xs, m + 1)
                        gate_or_up(m, 0, slab_of)
                        gate_or_up(m, 1, slab_of)
                        turn_hid(m)
                        down(m, slab_of)
            pe.nop()


_INS = ["x", "norm1_g", "w_in", "attn_sinks", "gmlp_ln_g", "gmlp_ln_b", "gmlp_ws", "gmlp_bs", "w_attn_branch",
        "w_gmlp_branch", "w_out", "norm2_g", "router_group_w", "router_group_b", "router_expert_w",
        "router_expert_b", "expert_w_gate", "expert_w_up", "expert_w_down", "final_norm_g"]


def kernel(**inputs):
    import concourse.bacc as _bacc
    from concourse.bass_utils import run_bass_kernel_spmd as _run

    nc = _bacc.Bacc("TRN2", target_bir_lowering=False, num_devices=1)
    arrays, args = {}, []
    turned = {"norm1_g": lambda a: a.reshape(KT, P).T, "gmlp_bs": lambda a: a[0].T,
              "attn_sinks": lambda a: a.reshape(KV_HEADS, PAIRS).T.reshape(1, HEADS)}
    given = [(name, np.ascontiguousarray(turned.get(name, lambda a: a)(np.asarray(inputs[name])))) for name in _INS]
    given += list(zip(("consts", "masks"), constants()))
    for name, a in given:
        arrays[f"in_{name}_dram"] = a
        args.append(nc.dram_tensor(f"in_{name}_dram", a.shape, mybir.dt.from_np(a.dtype), kind="ExternalInput").ap())
    args.append(nc.dram_tensor("out_0_dram", (1, SEQ, D), F32, kind="ExternalOutput").ap())
    build(nc, *args)
    result = _run(nc, [arrays], core_ids=[0])
    return result.results[0]["out_0_dram"]
```
